# Optimizing a Trainium2 kernel written in Bass

```python
import math
import jax
import jax.numpy as jnp
from jax import lax
import numpy as np

D_MODEL = 1024
BATCH = 1
SEQ = 1024
DEPTH = 2

D_MIX = D_MODEL
RMS_EPS = 1e-6

GLA_HEADS = 4
GLA_WIDTH = D_MIX // 2
GLA_DV = GLA_WIDTH // GLA_HEADS
GLA_DK = GLA_DV // 2
GLA_KDIM = GLA_HEADS * GLA_DK
GLA_GATE_RANK = 16
GLA_GATE_NORM = 16.0
GLA_CHUNK = 64

GMLP_HEADS = 4
GMLP_WIDTH = D_MIX // 4
GMLP_DH = GMLP_WIDTH // GMLP_HEADS
GMLP_CHUNK = 128

CONV_GROUPS = 4
CONV_WIDTH = D_MIX // 4
CONV_K = 3

PROJ_SIZES = (GLA_KDIM, GLA_KDIM, GLA_WIDTH, GLA_WIDTH, GLA_GATE_RANK,
              GMLP_WIDTH, GMLP_WIDTH,
              CONV_WIDTH, CONV_WIDTH, CONV_WIDTH)
D_IN = sum(PROJ_SIZES)

N_GROUPS = 4
EXPERTS_PER_GROUP = 8
N_EXPERTS = N_GROUPS * EXPERTS_PER_GROUP
TOP_K = 2
D_EXPERT = D_MODEL // 4
MOE_BLOCK = 128

kernel_name = "hymba_gla_gmlp_shortconv_hiermoe"

def rms_norm(x, gain):
    x32 = x.astype(jnp.float32)
    y = x32 * lax.rsqrt(jnp.mean(x32 * x32, axis=-1, keepdims=True) + RMS_EPS)
    return (y * gain.astype(jnp.float32)).astype(x.dtype)

def gla_mixer(q, k, v, g_out, gk_low, w_gk_up, b_gk, gla_norm):
    B, S, _ = q.shape
    N = S // GLA_CHUNK
    f32 = jnp.float32
    gk = jax.nn.log_sigmoid((gk_low @ w_gk_up + b_gk).astype(f32)) / GLA_GATE_NORM

    def to_chunks(t, d):
        return t.reshape(B, N, GLA_CHUNK, GLA_HEADS, d).transpose(0, 3, 1, 2, 4).astype(f32)

    qc = to_chunks(q, GLA_DK) * (GLA_DK ** -0.5)
    kc = to_chunks(k, GLA_DK)
    vc = to_chunks(v, GLA_DV)
    gc = to_chunks(gk, GLA_DK)
    b = jnp.cumsum(gc, axis=3)
    b_last = b[:, :, :, -1:, :]
    q_dec = qc * jnp.exp(b)
    k_inv = kc * jnp.exp(-b)
    k_dec = kc * jnp.exp(b_last - b)
    mask = jnp.tril(jnp.ones((GLA_CHUNK, GLA_CHUNK), dtype=bool))
    scores = jnp.where(mask, jnp.einsum('bhncd,bhnsd->bhncs', q_dec, k_inv), 0.0)
    o_intra = jnp.einsum('bhncs,bhnsv->bhncv', scores, vc)
    kv = jnp.einsum('bhncd,bhncv->nbhdv', k_dec, vc)
    decay = jnp.exp(b_last[:, :, :, 0, :]).transpose(2, 0, 1, 3)

    def step(state, inp):
        kv_n, d_n = inp
        return d_n[..., None] * state + kv_n, state

    s0 = jnp.zeros((B, GLA_HEADS, GLA_DK, GLA_DV), f32)
    _, s_prev = lax.scan(step, s0, (kv, decay))
    o_inter = jnp.einsum('bhncd,nbhdv->bhncv', q_dec, s_prev)
    o = (o_intra + o_inter).transpose(0, 2, 3, 1, 4).reshape(B, S, GLA_HEADS, GLA_DV)
    o = o * lax.rsqrt(jnp.mean(o * o, axis=-1, keepdims=True) + RMS_EPS) * gla_norm.astype(f32)
    gate = jax.nn.silu(g_out.astype(f32)).reshape(B, S, GLA_HEADS, GLA_DV)
    return (o * gate).reshape(B, S, GLA_WIDTH).astype(q.dtype)

def gmlp_mixer(u_raw, v_raw, gmlp_norm, w_spatial, b_spatial):
    B, S, _ = u_raw.shape
    N = S // GMLP_CHUNK
    shp = (B, N, GMLP_CHUNK, GMLP_HEADS, GMLP_DH)
    u = jax.nn.gelu(u_raw).reshape(shp)
    v32 = jax.nn.gelu(v_raw).reshape(shp).astype(jnp.float32)
    v32 = v32 * lax.rsqrt(jnp.mean(v32 * v32, axis=-1, keepdims=True) + RMS_EPS)
    v32 = v32 * gmlp_norm.reshape(GMLP_HEADS, GMLP_DH).astype(jnp.float32)
    mask = jnp.tril(jnp.ones((GMLP_CHUNK, GMLP_CHUNK), dtype=bool))
    w = jnp.where(mask[None], w_spatial, 0.0).astype(jnp.float32)
    mixed = jnp.einsum('hts,bnshd->bnthd', w, v32) + b_spatial.T.astype(jnp.float32)[:, :, None]
    return (u * mixed.astype(u.dtype)).reshape(B, S, GMLP_WIDTH)

def conv_mixer(x_in, b_gate, c_gate, w_conv):
    h = c_gate * x_in
    y = lax.conv_general_dilated(
        h, w_conv[:, None, :].astype(h.dtype), window_strides=(1,),
        padding=((CONV_K - 1, 0),), dimension_numbers=('NWC', 'WIO', 'NWC'),
        feature_group_count=CONV_WIDTH)
    return b_gate * y

def hier_moe(x2d, w_rg, b_rg, w_re, b_re, w_gate, w_up, w_down):
    T, D = x2d.shape
    f32 = jnp.float32
    g_logits = (x2d @ w_rg).astype(f32) + b_rg.astype(f32)
    g_prob = jax.nn.softmax(g_logits, axis=-1)
    g_top = jnp.argmax(g_logits, axis=-1)
    g_w = jnp.take_along_axis(g_prob, g_top[:, None], axis=-1)[:, 0]
    e_logits = ((x2d @ w_re).astype(f32) + b_re.astype(f32)).reshape(T, N_GROUPS, EXPERTS_PER_GROUP)
    e_in = jnp.take_along_axis(e_logits, g_top[:, None, None], axis=1)[:, 0]
    e_prob = jax.nn.softmax(e_in, axis=-1)
    top_p, top_i = lax.top_k(e_prob, TOP_K)
    weights = top_p / jnp.sum(top_p, axis=-1, keepdims=True) * g_w[:, None]
    expert_ids = g_top[:, None] * EXPERTS_PER_GROUP + top_i

    A = T * TOP_K
    e_flat = expert_ids.reshape(-1).astype(jnp.int32)
    t_flat = jnp.repeat(jnp.arange(T, dtype=jnp.int32), TOP_K)
    w_flat = weights.reshape(-1)
    order = jnp.argsort(e_flat)
    e_s, t_s, w_s = e_flat[order], t_flat[order], w_flat[order]
    counts = jnp.bincount(e_flat, length=N_EXPERTS)
    starts = jnp.cumsum(counts) - counts
    padded = (counts + MOE_BLOCK - 1) // MOE_BLOCK * MOE_BLOCK
    pend = jnp.cumsum(padded)
    pstarts = pend - padded
    dest = pstarts[e_s] + (jnp.arange(A, dtype=jnp.int32) - starts[e_s])
    P = ((A + MOE_BLOCK - 1) // MOE_BLOCK) * MOE_BLOCK + N_EXPERTS * MOE_BLOCK
    NB = P // MOE_BLOCK
    slot_tok = jnp.full((P,), T, dtype=jnp.int32).at[dest].set(t_s)
    slot_w = jnp.zeros((P,), f32).at[dest].set(w_s)
    block_start = jnp.arange(NB, dtype=jnp.int32) * MOE_BLOCK
    block_exp = jnp.minimum(jnp.sum(block_start[:, None] >= pend[None, :], axis=1), N_EXPERTS - 1)
    x_pad = jnp.concatenate([x2d, jnp.zeros((1, D), x2d.dtype)], axis=0)
    xb = x_pad[slot_tok].reshape(NB, MOE_BLOCK, D)

    def expert_block(args):
        xblk, e = args
        h = jax.nn.silu(xblk @ w_gate[e]) * (xblk @ w_up[e])
        return h @ w_down[e]

    yb = lax.map(expert_block, (xb, block_exp)).reshape(P, D)
    y = jax.ops.segment_sum(yb * slot_w[:, None].astype(yb.dtype), slot_tok, num_segments=T + 1)
    return y[:T]

def setup_inputs(seed: int = 0) -> dict:
    key = jax.random.key(seed)
    ks = jax.random.split(key, 24)
    L, D = DEPTH, D_MODEL

    def nrm(k, shape, scale):
        return jax.random.normal(k, shape, dtype=jnp.float32) * scale

    return {
        'x': nrm(ks[0], (BATCH, SEQ, D), 1.0),
        'attn_norm': 1.0 + nrm(ks[1], (L, D), 0.02),
        'w_in': nrm(ks[2], (L, D, D_IN), D ** -0.5),
        'w_gk_up': nrm(ks[3], (L, GLA_GATE_RANK, GLA_KDIM), GLA_GATE_RANK ** -0.5),
        'b_gk': nrm(ks[4], (L, GLA_KDIM), 0.1),
        'gla_norm': 1.0 + nrm(ks[5], (L, GLA_DV), 0.02),
        'gmlp_norm': 1.0 + nrm(ks[6], (L, GMLP_WIDTH), 0.02),
        'w_spatial': nrm(ks[7], (L, GMLP_HEADS, GMLP_CHUNK, GMLP_CHUNK), GMLP_CHUNK ** -0.5),
        'b_spatial': 1.0 + nrm(ks[8], (L, GMLP_HEADS, GMLP_CHUNK), 0.02),
        'w_conv': nrm(ks[9], (L, CONV_K, CONV_WIDTH), CONV_K ** -0.5),
        'w_out': nrm(ks[10], (L, D_MIX, D), D_MIX ** -0.5),
        'ffn_norm': 1.0 + nrm(ks[11], (L, D), 0.02),
        'w_router_group': nrm(ks[12], (L, D, N_GROUPS), D ** -0.5),
        'b_router_group': nrm(ks[13], (L, N_GROUPS), 0.01),
        'w_router_expert': nrm(ks[14], (L, D, N_EXPERTS), D ** -0.5),
        'b_router_expert': nrm(ks[15], (L, N_EXPERTS), 0.01),
        'w_gate': nrm(ks[16], (L, N_EXPERTS, D, D_EXPERT), D ** -0.5),
        'w_up': nrm(ks[17], (L, N_EXPERTS, D, D_EXPERT), D ** -0.5),
        'w_down': nrm(ks[18], (L, N_EXPERTS, D_EXPERT, D), D_EXPERT ** -0.5),
        'final_norm': 1.0 + nrm(ks[19], (D,), 0.02),
    }

def reference(x, attn_norm, w_in, w_gk_up, b_gk, gla_norm, gmlp_norm, w_spatial, b_spatial,
              w_conv, w_out, ffn_norm, w_router_group, b_router_group, w_router_expert,
              b_router_expert, w_gate, w_up, w_down, final_norm):
    B, S, D = x.shape
    split_points = []
    acc = 0
    for s in PROJ_SIZES[:-1]:
        acc += s
        split_points.append(acc)
    for l in range(DEPTH):
        h = rms_norm(x, attn_norm[l])
        proj = h @ w_in[l]
        q, k, v, g_out, gk_low, u, vg, x_in, b_gate, c_gate = jnp.split(proj, split_points, axis=-1)
        o_gla = gla_mixer(q, k, v, g_out, gk_low, w_gk_up[l], b_gk[l], gla_norm[l])
        o_gmlp = gmlp_mixer(u, vg, gmlp_norm[l], w_spatial[l], b_spatial[l])
        o_conv = conv_mixer(x_in, b_gate, c_gate, w_conv[l])
        mixed = jnp.concatenate([o_gla, o_gmlp, o_conv], axis=-1)
        x = x + mixed @ w_out[l]
        h = rms_norm(x, ffn_norm[l]).reshape(B * S, D)
        y = hier_moe(h, w_router_group[l], b_router_group[l], w_router_expert[l], b_router_expert[l],
                     w_gate[l], w_up[l], w_down[l])
        x = x + y.reshape(B, S, D)
    return rms_norm(x, final_norm)


_drawn_inputs = setup_inputs


def setup_inputs(seed=0):
    import zlib

    import numpy as np

    out = dict(_drawn_inputs(seed))
    spreads = {}
    factors = {}
    for name, (base, spread) in spreads.items():
        noise = np.random.default_rng([zlib.crc32(name.encode()), seed]).standard_normal(out[name].shape)
        drawn = base * np.exp(spread * noise) if base else spread * noise
        out[name] = jnp.asarray(drawn.astype(out[name].dtype))
    for name, factor in factors.items():
        out[name] = (out[name] * factor).astype(out[name].dtype)
    return out
```

```python
from contextlib import ExitStack

import concourse.bass as bass
from concourse import mybir

F32 = mybir.dt.float32
F32R = mybir.dt.float32r
BF16 = mybir.dt.bfloat16
I32 = mybir.dt.int32
ALU = mybir.AluOpType
ACT = mybir.ActivationFunctionType
AX_X = mybir.AxisListType.X

P = 128
EPS = 1e-6
BANK = 512

GLA_HEADS, DK, DV, RANK, CHUNK = 4, 64, 128, 16, 64
KDIM, GLA_W = GLA_HEADS * DK, GLA_HEADS * DV
GATE_NORM = 16.0
GM_HEADS, GM_DH, GM_W = 4, 64, 256
CONV_W, CONV_K = 256, 3
COL_Q, COL_V = 0, 2 * KDIM
COL_G = COL_V + GLA_W
COL_GK = COL_G + GLA_W
COL_VG = COL_GK + RANK + GM_W
COL_CONV = COL_VG + GM_W

N_GROUPS, PER_GROUP = 4, 8
N_EXP = N_GROUPS * PER_GROUP
TOP_K = 2
EMPTY = 8192.0


def build(nc, x, attn_norm, w_in, w_gk_up, b_gk, gla_norm, gmlp_norm, w_spatial, b_spatial, w_conv,
          w_out, ffn_norm, ffn_norm_col, w_router_group, b_router_group, w_router_expert, b_router_expert,
          w_gate, w_up, w_down, final_norm, out):
    DEPTH = attn_norm.shape[0]
    _, SEQ, D = x.shape
    DX = w_gate.shape[3]
    KT = D // P
    NT = SEQ // P
    HALVES = 2
    HT_ = NT // HALVES
    HTOK = HT_ * P
    NCH = HTOK // CHUNK
    ASSIGN = SEQ * TOP_K
    NBLK = ASSIGN // P + N_EXP
    NCOL = NBLK + 3
    assert HTOK == BANK and D == 1024 and DX == 256

    x_rows = x.rearrange("b (j p) d -> p (b j) d", p=P)
    out_rows = out.rearrange("b (j p) d -> p (b j) d", p=P)
    h_dram = nc.dram_tensor("h_rows", (SEQ, D), F32, kind="Internal").ap()
    y_dram = nc.dram_tensor("y_rows", (ASSIGN, D), F32, kind="Internal").ap()
    y_view = y_dram.rearrange("(k j p) d -> j p k d", k=TOP_K, p=P)

    with ExitStack() as whole:
        def sb(name, shape, dt=F32, ctx=whole):
            return ctx.enter_context(nc.sbuf_tensor(name, shape, dt))

        X = sb("X", [P, NT, D])
        ident = sb("ident", [P, P])
        causal = sb("causal", [P, P], I32)
        scan_keep = sb("scan_keep", [P, 2 * HTOK])
        before = sb("before", [P, P])
        ones = sb("ones", [P, P])
        iota_row = sb("iota_row", [P, P])
        tok1 = sb("tok1", [P, 1])
        q_map = sb("q_map", [P, NT, TOP_K])
        minus_half = sb("minus_half", [P, 16])
        row_ss = sb("row_ss", [P, NT])
        row_rstd = sb("row_rstd", [P, NT])
        state = sb("state", [P, NCH + 1, 2, DV])
        halo = sb("halo", [P, 2, CONV_K - 1])
        Wtok = sb("Wtok", [P, NT, TOP_K])
        slot_tok = sb("slot_tok", [P, NCOL], I32)
        slot_row = sb("slot_row", [P, NCOL], I32)
        blk_exp = sb("blk_exp", [1, NCOL], I32)
        last_pair = sb("last_pair", [P, 1], I32)

        banks = [whole.enter_context(nc.psum_tensor(f"bank{i}", [P, BANK], F32)) for i in range(8)]

        def phase(sems, programs):
            with nc.Block() as block:
                programs(block)
            numbers = sorted(s.num for s in sems)
            nc.all_engine_barrier(sems_to_clear=range(numbers[0], numbers[-1] + 1))

        def chain(eng, sem):
            count = [0]

            def link(ins):
                count[0] += 1
                ins.then_inc(sem, 1)
                eng.wait_ge(sem, count[0])
            return link

        def square_rows(act, sq, j, sumsq):
            if j:
                act.wait_ge(sumsq, j)
            nc.scalar.activation(sq[:], X[:, j, :], ACT.Square, accum_out=row_ss[:, j:j + 1]).then_inc(sumsq, 1)

        def mean_squares(dve, sumsq, ready):
            dve.wait_ge(sumsq, NT)
            nc.vector.tensor_scalar(row_ss[:], row_ss[:], 1.0 / D, EPS, ALU.mult, ALU.add).then_inc(ready, 1)

        def row_rstds(pool, mean_ready, done):
            pool.wait_ge(mean_ready, 1)
            nc.gpsimd.tensor_tensor(row_rstd[:], row_ss[:], minus_half[:, 0:NT], ALU.pow).then_inc(done, 1)

        def reset_state(pool, done):
            nc.gpsimd.memset(state[:, 0], 0.0).then_inc(done, 1)
            nc.gpsimd.memset(halo[:], 0.0).then_inc(done, 1)

        with ExitStack() as ctx:
            s_x = [ctx.enter_context(nc.semaphore(f"x_loaded{j}")) for j in range(NT)]
            s_pool = ctx.enter_context(nc.semaphore("pool_step"))
            s_sumsq, s_mean = (ctx.enter_context(nc.semaphore(n)) for n in ("sumsq0", "mean_square0"))
            sq = sb("sq0", [P, D], F32, ctx)

            def setup(block):
                @block.sync
                def _(sp):
                    for j in range(NT):
                        sp.dma_start(X[:, j, :], x_rows[:, j, :]).then_inc(s_x[j], 16)

                @block.scalar
                def _(act):
                    for j in range(NT):
                        act.wait_ge(s_x[j], 16)
                        square_rows(act, sq, j, s_sumsq)

                @block.vector
                def _(dve):
                    mean_squares(dve, s_sumsq, s_mean)

                @block.gpsimd
                def _(pool):
                    link = chain(pool, s_pool)
                    g = nc.gpsimd
                    link(g.memset(ident[:], 0.0))
                    link(g.affine_select(out=ident[:], in_=ident[:], compare_op=ALU.not_equal, fill=1.0, base=0,
                                         pattern=[[-1, P]], channel_multiplier=1))
                    link(g.memset(ones[:], 1.0))
                    link(g.memset(causal[:], 0))
                    for c in range(P // CHUNK):
                        part = slice(c * CHUNK, (c + 1) * CHUNK)
                        link(g.affine_select(out=causal[part, part], in_=causal[part, part], compare_op=ALU.is_gt,
                                             fill=1.0, base=0, pattern=[[-1, CHUNK]], channel_multiplier=1))
                    link(g.affine_select(out=before[:], in_=ones[:], compare_op=ALU.is_ge, fill=0.0, base=-1,
                                         pattern=[[1, P]], channel_multiplier=-1))
                    link(g.memset(scan_keep[:], 1.0))
                    link(g.memset(scan_keep[:].rearrange("p (n c) -> p n c", c=CHUNK)[:, :, 0:1], 0.0))
                    link(g.iota(iota_row[:], pattern=[[1, P]], base=0, channel_multiplier=0,
                                allow_small_or_imprecise_dtypes=True))
                    link(g.iota(tok1[:], pattern=[[0, 1]], base=1, channel_multiplier=1,
                                allow_small_or_imprecise_dtypes=True))
                    link(g.iota(q_map[:], pattern=[[1, NT], [NT, TOP_K]], base=0, channel_multiplier=0,
                                allow_small_or_imprecise_dtypes=True))
                    link(g.memset(minus_half[:], -0.5))
                    reset_state(pool, s_pool)
                    row_rstds(pool, s_mean, s_pool)

            phase(s_x + [s_pool, s_sumsq, s_mean], setup)

        def mixer_half(L, half):
            with ExitStack() as ctx:
                RAW, SPLIT = 4, 5
                ON_ACT = 1
                local = lambda name, shape, dt=F32: sb(name, shape, dt, ctx)
                hT_hi = local("hT_hi", [P, KT, HTOK], F32R)
                hT_lo = local("hT_lo", [P, KT, HTOK], F32R)
                mT_hi = local("mT_hi", [P, KT, HTOK], F32R)
                mT_lo = local("mT_lo", [P, KT, HTOK], F32R)
                w_raw = local("w_raw", [P, RAW, BANK])
                w_hi = local("w_hi", [P, SPLIT, BANK], F32R)
                w_lo = local("w_lo", [P, SPLIT, BANK], F32R)
                xn = local("xn", [P, HT_, D])
                V = xn[:].rearrange("p a b -> p (a b)")[:, 0:HT_ * GLA_W].rearrange("p (i c) -> p i c", i=HT_)
                GG = xn[:].rearrange("p a b -> p (a b)")[:, HT_ * GLA_W:].rearrange("p (i c) -> p i c", i=HT_)
                Q = local("Q", [P, 2, HTOK])
                K = local("K", [P, 2, HTOK])
                Z = local("Z", [P, 2, HTOK])
                E1 = local("E1", [P, 2, HTOK])
                E2 = local("E2", [P, 2, HTOK])
                KD = E2[:].rearrange("p f t -> p (f t)").rearrange("p (i c) -> p i c", i=HT_)
                U = local("U", [P, HT_, GM_W])
                VG = local("VG", [P, HT_, GM_W])
                O = local("O", [P, HT_, GLA_W])
                SQ = local("SQ", [P, D])
                glT = SQ[0:RANK, 0:HTOK]
                PT = local("PT", [P, GLA_HEADS, P])
                wspT = local("wspT", [P, GM_HEADS, P])
                GL = local("GL", [P, HT_, RANK])
                Hc = local("Hc", [P, CONV_K - 1 + HTOK])
                gain_col = local("gain_col", [P, KT])
                gk_up = local("gk_up", [RANK, KDIM])
                gk_bias = local("gk_bias", [P, 2])
                gla_gain = local("gla_gain", [P, 1])
                gm_gain = local("gm_gain", [P, GM_W])
                sp_bias = local("sp_bias", [P, GM_HEADS])
                cw = local("cw", [P, 2, CONV_K])
                hs = local("hs", [P, HT_ * GLA_HEADS])
                hr = local("hr", [P, HT_ * GLA_HEADS])
                gs = local("gs", [P, HT_ * GM_HEADS])
                gr = local("gr", [P, HT_ * GM_HEADS])

                sems = []

                def sem(name):
                    sems.append(ctx.enter_context(nc.semaphore(name)))
                    return sems[-1]

                def x_tile(i):
                    return X[:, bass.ds(half * HT_ + i, 1), :].rearrange("p a d -> p (a d)")

                def rstd_of(i):
                    return row_rstd[:, bass.ds(half * HT_ + i, 1)]

                param = {n: sem(f"{n}_loaded") for n in ("gain", "gk", "gla", "gm", "spw", "spb", "conv")}
                raw_loaded = [sem(f"raw_loaded{i}") for i in range(RAW)]
                w_hi_ready, w_lo_ready = sem("w_hi_ready"), sem("w_lo_ready")
                chunk_used = sem("chunk_used")
                tile_ready = sem("tile_ready")
                bank_read = [sem(f"bank_read{i}") for i in range(8)]
                act_step, dve_step = sem("act_step"), sem("dve_step")
                xn_act, xn_dve, hT_tr, hT_hi_ready = sem("xn_act"), sem("xn_dve"), sem("hT_transposed"), sem("hT_hi_ready")
                sp_masked = sem("sp_masked")
                gl_ready, gl_tr, gk_ready = sem("gl_ready"), sem("gl_transposed"), sem("gk_ready")
                abs_ready, soft_ready = sem("abs_ready"), sem("soft_ready")
                cum_ready, exp_ready, gated = sem("cum_ready"), sem("exp_ready"), sem("qk_gated")
                kd_tr, scores, kv_done, o_done = sem("kd_transposed"), sem("scores"), sem("kv_done"), sem("o_done")
                head_ms, head_rstd, og_ready = sem("head_ms"), sem("head_rstd"), sem("og_ready")
                og_tr, m_hi_ready = sem("og_transposed"), sem("m_hi_ready")
                vg_ms, vg_rstd, vg_normed = sem("vg_ms"), sem("vg_rstd"), sem("vg_normed")
                mixed, um_tr, conv_split = sem("spatial_mixed"), sem("um_transposed"), sem("conv_split")

                ROW, COLT = "row", "col"
                GROUPS = [("gk_u", ROW, HT_, RANK + GM_W), ("qk", COLT, 4, 4 * P), ("v", ROW, HT_, GLA_W),
                          ("g", ROW, HT_, GLA_W), ("vg", ROW, HT_, GM_W), ("conv0", COLT, 3, 3 * P),
                          ("conv1", COLT, 3, 3 * P), ("out0", ROW, HT_, BANK), ("out1", ROW, HT_, BANK)]
                first_col = {"gk_u": COL_GK, "qk": COL_Q, "v": COL_V, "g": COL_G, "vg": COL_VG}
                OUT_K = [6, 0, 1, 2, 3, 7, 4, 5]
                first_tile, t = {}, 0
                for name, _, tiles, _ in GROUPS:
                    first_tile[name] = t
                    t += tiles
                chunks = [(name, kind, k, ncols) for name, kind, _, ncols in GROUPS for k in range(KT)]
                RING = 6
                bank_of = lambda tile: banks[tile % RING]
                tiles_of = {g[0]: g[2] for g in GROUPS}
                group_no = {g[0]: n for n, g in enumerate(GROUPS)}
                per_tile = [f"{n}{i}" for i in range(HT_) for n in ("sc", "kv", "o")]
                order6 = ["hT6", "glT", "gk1", "kd0"] + per_tile + ["ogT0", "ogT2", "mix0", "umT0"]
                order7 = ["hT7", "gk0", "kd1"] + per_tile + ["ogT1", "ogT3", "mix1", "umT1"]

                def tile_done(eng, name, j):
                    if j == tiles_of[name] - 1:
                        eng.wait_ge(chunk_used, KT * (group_no[name] + 1))
                    else:
                        eng.wait_ge(tile_ready, first_tile[name] - group_no[name] + j + 1)

                def tile_read(eng, name, j):
                    t = first_tile[name] + j
                    eng.wait_ge(bank_read[t % RING], t // RING + 2)

                def mixer_read(eng, b, use):
                    eng.wait_ge(bank_read[b], (order6 if b == 6 else order7).index(use) + 1)

                def chunk_source(name, k):
                    if name.startswith("out"):
                        c0 = BANK * int(name[3])
                        rows = OUT_K[k]
                        return w_out[bass.ds(L, 1), rows * P:(rows + 1) * P, c0:c0 + BANK].rearrange("a p c -> (a p) c")
                    rows = w_in[bass.ds(L, 1), k * P:(k + 1) * P, :]
                    if name.startswith("conv"):
                        f = int(name[4])
                        return rows[:, :, COL_CONV:].rearrange("a p (j c) -> (a p) j c", j=3)[:, :, f * P:(f + 1) * P]
                    c0 = first_col[name]
                    n = {g[0]: g[3] for g in GROUPS}[name]
                    return rows[:, :, c0:c0 + n].rearrange("a p c -> (a p) c")

                def mixer(block):
                    @block.sync
                    def _(sp):
                        sp.dma_start(gain_col[:], attn_norm[bass.ds(L, 1)].rearrange("a p k -> (a p) k")
                                     ).then_inc(param["gain"], 16)
                        for n, (name, kind, k, ncols) in enumerate(chunks):
                            if n >= RAW:
                                sp.wait_ge(w_lo_ready, n - RAW + 1)
                            dst = w_raw[:, n % RAW, 0:ncols]
                            if name.startswith("conv"):
                                dst = dst.rearrange("p (j c) -> p j c", j=3)
                            sp.dma_start(dst, chunk_source(name, k)).then_inc(raw_loaded[n % RAW], 16)
                            if n == RAW - 1:
                                sp.dma_start(wspT[:], w_spatial[bass.ds(L, 1)].rearrange("a s h t -> (a s) h t")
                                             ).then_inc(param["spw"], 16)
                                sp.dma_start(gk_up[:], w_gk_up[bass.ds(L, 1)].rearrange("a r c -> (a r) c")
                                             ).then_inc(param["gk"], 16)
                                sp.dma_start(gk_bias[:], b_gk[bass.ds(L, 1)].rearrange("a p f -> (a p) f")
                                             ).then_inc(param["gk"], 16)
                                sp.dma_start(gla_gain[:], gla_norm[bass.ds(L, 1)].rearrange("a p b -> (a p) b")
                                             ).then_inc(param["gla"], 16)
                                sp.dma_start(gm_gain[:], gmlp_norm[bass.ds(L, 1), :].broadcast_to([P, GM_W])
                                             ).then_inc(param["gm"], 16)
                                sp.dma_start(sp_bias[:], b_spatial[bass.ds(L, 1)].rearrange("a t h -> (a t) h")
                                             ).then_inc(param["spb"], 16)
                                sp.dma_start(cw[:], w_conv[bass.ds(L, 1)].rearrange("a p f j -> (a p) f j")
                                             ).then_inc(param["conv"], 16)

                    @block.gpsimd
                    def _(pool):
                        g = nc.gpsimd

                        def split(n):
                            ncols = chunks[n][3]
                            raw = w_raw[:, n % RAW, 0:ncols]
                            hi = w_hi[:, n % SPLIT, 0:ncols]
                            pool.wait_ge(w_hi_ready, n + 1)
                            g.tensor_tensor(w_lo[:, n % SPLIT, 0:ncols], raw, hi.bitcast(F32),
                                            ALU.subtract).then_inc(w_lo_ready, 1)

                        for n in range(SPLIT):
                            split(n)
                        pool.wait_ge(param["spw"], 16)
                        g.affine_select(out=wspT[:], in_=wspT[:], compare_op=ALU.is_ge, fill=0.0, base=0,
                                        pattern=[[0, GM_HEADS], [1, P]], channel_multiplier=-1).then_inc(sp_masked, 1)
                        for n in range(SPLIT, len(chunks)):
                            if (chunks[n][0], chunks[n][2]) == ("conv0", 4):
                                pool.wait_ge(head_ms, 1)
                                g.tensor_tensor(hr[:], hs[:], minus_half[:, 0:HT_ * GLA_HEADS],
                                                ALU.pow).then_inc(head_rstd, 1)
                            if (chunks[n][0], chunks[n][2]) == ("conv0", 6):
                                pool.wait_ge(vg_ms, 1)
                                g.tensor_tensor(gr[:], gs[:], minus_half[:, 0:HT_ * GM_HEADS],
                                                ALU.pow).then_inc(vg_rstd, 1)
                            split(n)

                    @block.tensor
                    def _(pe):
                        mm, tr = nc.tensor.matmul, nc.tensor.transpose

                        def claim(b, name):
                            uses = (order6 if b == 6 else order7).index(name)
                            if uses:
                                pe.wait_ge(bank_read[b], uses)

                        pe.wait_ge(xn_act, ON_ACT)
                        pe.wait_ge(xn_dve, HT_ - ON_ACT)
                        for k in range(KT):
                            for i in range(HT_):
                                ins = tr(banks[k][:, i * P:(i + 1) * P], xn[:, i, k * P:(k + 1) * P], ident[:])
                            ins.then_inc(hT_tr, 1)

                        def gl_transpose():
                            claim(6, "glT")
                            pe.wait_ge(gl_ready, HT_)
                            for i in range(HT_):
                                ins = tr(banks[6][0:RANK, i * P:(i + 1) * P], GL[:, i, :], ident[:])
                            ins.then_inc(gl_tr, 1)

                        def gate_logits():
                            pe.wait_ge(param["gk"], 32)
                            mixer_read(pe, 6, "glT")
                            for f in range(2):
                                claim(7 - f, f"gk{f}")
                                mm(banks[7 - f][:], gk_up[:, f * P:(f + 1) * P], glT, start=True,
                                   stop=True).then_inc(gk_ready, 1)

                        def kd_transpose():
                            pe.wait_ge(gated, 3)
                            for b in range(2):
                                claim(6 + b, f"kd{b}")
                                for i in range(2):
                                    for f in range(2):
                                        tt = 2 * b + i
                                        ins = tr(banks[6 + b][:, (2 * i + f) * P:(2 * i + f + 1) * P],
                                                 Z[:, f, tt * P:(tt + 1) * P], ident[:])
                                ins.then_inc(kd_tr, 1)

                        def score_tile(i):
                            toks = slice(i * P, (i + 1) * P)
                            claim(6, f"sc{i}")
                            claim(7, f"sc{i}")
                            for h in range(GLA_HEADS):
                                part = slice(DK * (h % 2), DK * (h % 2) + DK)
                                ins = mm(banks[6 + h % 2][:, (h // 2) * P:(h // 2 + 1) * P], K[part, h // 2, toks],
                                         Q[part, h // 2, toks], start=True, stop=True)
                            ins.then_inc(scores, 1)

                        def kv_tile(i):
                            claim(6, f"kv{i}")
                            claim(7, f"kv{i}")
                            mixer_read(pe, 6 + i // 2, f"kd{i // 2}")
                            tile_read(pe, "v", i)
                            for h in range(GLA_HEADS):
                                part = slice(DK * (h % 2), DK * (h % 2) + DK)
                                for c in range(2):
                                    rows = slice(c * CHUNK, (c + 1) * CHUNK)
                                    ins = mm(banks[6 + c][part, (h // 2) * DV:(h // 2 + 1) * DV],
                                             KD[rows, i, h * DK:(h + 1) * DK], V[rows, i, h * DV:(h + 1) * DV],
                                             start=True, stop=True)
                            ins.then_inc(kv_done, 1)

                        def out_tile(i):
                            claim(6, f"o{i}")
                            claim(7, f"o{i}")
                            for h in range(GLA_HEADS):
                                part = slice(DK * (h % 2), DK * (h % 2) + DK)
                                cols = slice((h // 2) * DV, (h // 2 + 1) * DV)
                                mm(banks[6 + h % 2][:, cols], PT[:, h, :], V[:, i, h * DV:(h + 1) * DV],
                                   start=True, stop=False)
                                for c in range(2):
                                    rows = slice(c * CHUNK, (c + 1) * CHUNK)
                                    t0 = i * P + c * CHUNK
                                    ins = mm(banks[6 + h % 2][rows, cols], Q[part, h // 2, t0:t0 + CHUNK],
                                             state[part, 2 * i + c, h // 2, :], start=False, stop=True)
                            ins.then_inc(o_done, 1)

                        def og_transpose(h):
                            if h == 0:
                                pe.wait_ge(og_ready, HT_)
                            claim(6 + h % 2, f"ogT{h}")
                            for i in range(HT_):
                                ins = tr(banks[6 + h % 2][:, i * P:(i + 1) * P], O[:, i, h * DV:(h + 1) * DV], ident[:])
                            ins.then_inc(og_tr, 1)

                        def spatial_mix():
                            pe.wait_ge(sp_masked, 1)
                            pe.wait_ge(vg_normed, 1)
                            for i in range(HT_):
                                b = 6 + i // 2
                                if i % 2 == 0:
                                    claim(b, f"mix{i // 2}")
                                for h in range(GM_HEADS):
                                    at = (i % 2) * GM_W + h * GM_DH
                                    ins = mm(banks[b][:, at:at + GM_DH], wspT[:, h, :],
                                             VG[:, i, h * GM_DH:(h + 1) * GM_DH], start=True, stop=True)
                                if i % 2:
                                    ins.then_inc(mixed, 1)

                        def um_transpose():
                            for b in range(2):
                                mixer_read(pe, 6 + b, f"mix{b}")
                            for f in range(2):
                                claim(6 + f, f"umT{f}")
                                for i in range(HT_):
                                    ins = tr(banks[6 + f][:, i * P:(i + 1) * P], U[:, i, f * P:(f + 1) * P], ident[:])
                                ins.then_inc(um_tr, 1)

                        between = {("qk", 2): gl_transpose, ("qk", 3): gate_logits, ("v", 6): kd_transpose,
                                   ("conv1", 6): spatial_mix, ("out0", 2): um_transpose}
                        for h in range(GLA_HEADS):
                            between[("conv1", h + 1)] = lambda h=h: og_transpose(h)
                        gla_slots = [("g", k) for k in range(KT)] + [("vg", k) for k in (1, 3, 5, 7)]
                        gla_steps = [(f, i) for i in range(HT_) for f in (score_tile, kv_tile, out_tile)]
                        for slot, (f, i) in zip(gla_slots, gla_steps):
                            between[slot] = lambda f=f, i=i: f(i)

                        n = 0
                        for name, kind, tiles, ncols in GROUPS:
                            src_hi, src_lo = (mT_hi, mT_lo) if name.startswith("out") else (hT_hi, hT_lo)
                            for kk in range(KT):
                                k = OUT_K[kk] if name.startswith("out") else kk
                                if (name, kk) in between:
                                    between[(name, kk)]()
                                pe.wait_ge(w_lo_ready, n + 1)
                                if name == "gk_u":
                                    pe.wait_ge(bank_read[kk], 1)
                                if name == "out0":
                                    if k < 4:
                                        mixer_read(pe, 6 + k % 2, f"ogT{k}")
                                    elif k < 6:
                                        mixer_read(pe, 2 + k, f"umT{k - 4}")
                                    else:
                                        pe.wait_ge(conv_split, k - 5)
                                hi, lo = w_hi[:, n % SPLIT, :], w_lo[:, n % SPLIT, :]
                                for j in range(tiles):
                                    tile = first_tile[name] + j
                                    if kk == 0:
                                        pe.wait_ge(bank_read[tile % RING], tile // RING + 1)
                                    dst = bank_of(tile)
                                    if kind == ROW:
                                        toks = slice(j * P, (j + 1) * P)
                                        dst = dst[:, 0:ncols]
                                        pairs = [(src_hi[:, k, toks], hi[:, 0:ncols]), (src_hi[:, k, toks], lo[:, 0:ncols]),
                                                 (src_lo[:, k, toks], hi[:, 0:ncols])]
                                    else:
                                        cols = slice(j * P, (j + 1) * P)
                                        dst = dst[:]
                                        pairs = [(hi[:, cols], src_hi[:, k, :]), (hi[:, cols], src_lo[:, k, :]),
                                                 (lo[:, cols], src_hi[:, k, :])]
                                    for m, (a, b) in enumerate(pairs):
                                        ins = mm(dst, a, b, start=(kk == 0 and m == 0), stop=(kk == KT - 1 and m == 2))
                                    if kk == KT - 1 and j < tiles - 1:
                                        ins.then_inc(tile_ready, 1)
                                ins.then_inc(chunk_used, 1)
                                n += 1

                    @block.scalar
                    def _(act):
                        link = chain(act, act_step)
                        a = nc.scalar.activation
                        at = lambda name, k: KT * group_no[name] + k
                        emitted = [0]

                        def high_to(name, k):
                            for n in range(emitted[0], at(name, k) + 1):
                                act.wait_ge(raw_loaded[n % RAW], 16 * (n // RAW + 1))
                                if n >= SPLIT:
                                    act.wait_ge(chunk_used, n - SPLIT + 1)
                                ncols = chunks[n][3]
                                a(w_hi[:, n % SPLIT, 0:ncols], w_raw[:, n % RAW, 0:ncols], ACT.Copy).then_inc(w_hi_ready, 1)
                                emitted[0] = n + 1

                        for i in range(ON_ACT):
                            a(xn[:, i, :], x_tile(i), ACT.Copy, scale=rstd_of(i)).then_inc(xn_act, 1)
                        high_to("gk_u", RAW - 1)
                        act.wait_ge(param["gain"], 16)
                        for k in range(KT):
                            act.wait_ge(hT_tr, k + 1)
                            a(hT_hi[:, k, :], banks[k][:], ACT.Copy, scale=gain_col[:, k:k + 1]).then_inc(hT_hi_ready, 1)
                            if k == KT // 2:
                                high_to("gk_u", SPLIT - 1)

                        def tile_out(dst, name, j, func, cols=slice(0, BANK)):
                            t = first_tile[name] + j
                            a(dst, bank_of(t)[:, cols], func).then_inc(bank_read[t % RING], 1)

                        high_to("qk", 2)
                        for i in range(HT_):
                            tile_done(act, "gk_u", i)
                            a(GL[:, i, :], bank_of(first_tile["gk_u"] + i)[:, 0:RANK], ACT.Copy).then_inc(gl_ready, 1)
                            tile_out(U[:, i, :], "gk_u", i, ACT.Gelu_apprx_tanh, slice(RANK, RANK + GM_W))
                        high_to("qk", 5)
                        act.wait_ge(gl_tr, 1)
                        a(glT, banks[6][0:RANK, :], ACT.Copy).then_inc(bank_read[6], 1)
                        high_to("qk", 6)
                        act.wait_ge(abs_ready, 1)
                        link(a(E1[:], E2[:], ACT.Exp))
                        a(E2[:], E1[:], ACT.Ln, bias=1.0).then_inc(soft_ready, 1)
                        high_to("v", 2)
                        for j in range(4):
                            tile_done(act, "qk", j)
                            tile_out((Q if j < 2 else K)[:, j % 2, :], "qk", j, ACT.Copy)
                        high_to("v", 3)
                        act.wait_ge(cum_ready, 1)
                        a(E1[:], Z[:], ACT.Exp, scale=1.0 / GATE_NORM).then_inc(exp_ready, 1)
                        a(E2[:], Z[:], ACT.Exp, scale=-1.0 / GATE_NORM).then_inc(exp_ready, 1)
                        high_to("g", 0)
                        for b in range(2):
                            act.wait_ge(kd_tr, b + 1)
                            a(KD[:, 2 * b:2 * b + 2, :].rearrange("p i c -> p (i c)"), banks[6 + b][:],
                              ACT.Copy).then_inc(bank_read[6 + b], 1)
                        high_to("g", 3)
                        for i in range(HT_):
                            tile_done(act, "v", i)
                            tile_out(V[:, i, :], "v", i, ACT.Copy)

                        def o_out(i):
                            act.wait_ge(o_done, i + 1)
                            for b in range(2):
                                a(O[:, i, :].rearrange("p (a b c) -> p b a c", b=2, c=DV)[:, b],
                                  banks[6 + b][:, 0:2 * DV].rearrange("p (a c) -> p a c", c=DV), ACT.Copy
                                  ).then_inc(bank_read[6 + b], 1)

                        high_to("g", 5)
                        o_out(0)
                        high_to("vg", 0)
                        o_out(1)
                        high_to("vg", 2)
                        for i in range(HT_):
                            tile_done(act, "g", i)
                            tile_out(GG[:, i, :], "g", i, ACT.Silu)
                        high_to("vg", 4)
                        o_out(2)
                        high_to("conv0", 2)
                        o_out(3)
                        high_to("conv0", 3)
                        for i in range(HT_):
                            tile_done(act, "vg", i)
                            tile_out(VG[:, i, :], "vg", i, ACT.Gelu_apprx_tanh, slice(0, GM_W))

                        def conv_out(f):
                            tile_done(act, f"conv{f}", 0)
                            if f == 0:
                                act.wait_ge(vg_ms, 1)
                            else:
                                tile_read(act, "conv0", 2)
                            tile_out(SQ[:, 0:HTOK], f"conv{f}", 0, ACT.Copy)
                            tile_read(act, f"conv{f}", 1)
                            a(mT_hi[:, 6 + f, :], Z[:, f, :], ACT.Copy).then_inc(m_hi_ready, 1)

                        high_to("conv1", 2)
                        conv_out(0)
                        act.wait_ge(param["gla"], 16)
                        for h in range(GLA_HEADS):
                            high_to("conv1", 3 + h)
                            act.wait_ge(og_tr, h + 1)
                            a(mT_hi[:, h, :], banks[6 + h % 2][:], ACT.Copy, scale=gla_gain[:]).then_inc(m_hi_ready, 1)
                        high_to("out0", 2)
                        conv_out(1)
                        high_to("out0", 5)
                        for f in range(2):
                            act.wait_ge(um_tr, f + 1)
                            a(mT_hi[:, 4 + f, :], banks[6 + f][:], ACT.Copy).then_inc(m_hi_ready, 1)
                        high_to("out1", KT - 1)

                    @block.vector
                    def _(dve):
                        link = chain(dve, dve_step)
                        v = nc.vector
                        flat = lambda t: t[:].rearrange("p a b -> p (a b)")
                        for i in range(ON_ACT, HT_):
                            v.tensor_scalar(xn[:, i, :], x_tile(i), rstd_of(i), None, ALU.mult).then_inc(xn_dve, 1)
                        dve.wait_ge(param["gain"], 16)
                        for k in range(KT):
                            dve.wait_ge(hT_hi_ready, k + 1)
                            v.scalar_tensor_tensor(out=hT_lo[:, k, :], in0=banks[k][:], scalar=gain_col[:, k:k + 1],
                                                   in1=hT_hi[:, k, :].bitcast(F32), op0=ALU.mult, op1=ALU.subtract
                                                   ).then_inc(bank_read[k], 1)
                        dve.wait_ge(param["gk"], 32)
                        for f in range(2):
                            dve.wait_ge(gk_ready, f + 1)
                            v.tensor_scalar(Z[:, f, :], banks[7 - f][:], gk_bias[:, f:f + 1], None, ALU.add
                                            ).then_inc(bank_read[7 - f], 1)
                        mixer_read(dve, 7, "gk0")
                        mixer_read(dve, 6, "gk1")
                        v.scalar_tensor_tensor(out=flat(E2), in0=flat(Z), scalar=-1.0, in1=flat(Z), op0=ALU.mult,
                                               op1=ALU.min).then_inc(abs_ready, 1)
                        dve.wait_ge(soft_ready, 1)
                        link(v.scalar_tensor_tensor(out=flat(E1), in0=flat(Z), scalar=0.0, in1=flat(E2), op0=ALU.min,
                                                    op1=ALU.subtract))
                        v.tensor_tensor_scan(flat(Z), scan_keep[:], flat(E1), 0.0, ALU.mult, ALU.add
                                             ).then_inc(cum_ready, 1)
                        for j in range(4):
                            tile_read(dve, "qk", j)
                        dve.wait_ge(exp_ready, 1)
                        v.scalar_tensor_tensor(out=flat(Q), in0=flat(Q), scalar=DK ** -0.5, in1=flat(E1),
                                               op0=ALU.mult, op1=ALU.mult).then_inc(gated, 1)
                        dve.wait_ge(exp_ready, 2)
                        v.tensor_tensor(flat(K), flat(K), flat(E2), ALU.mult).then_inc(gated, 1)
                        dve.wait_ge(gated, 2)
                        by_chunk = lambda t: t[:].rearrange("p f (n c) -> p (f n) c", c=CHUNK)
                        v.tensor_tensor(by_chunk(Z), by_chunk(K),
                                        by_chunk(E1)[:, :, CHUNK - 1:CHUNK].broadcast_to([P, 2 * NCH, CHUNK]),
                                        ALU.mult).then_inc(gated, 1)
                        link(v.memset(PT[:], 0.0))
                        causal2 = causal[:].unsqueeze(1).broadcast_to([P, 2, P])

                        def head_squares(i):
                            for b in range(2):
                                mixer_read(dve, 6 + b, f"o{i}")
                            link(v.tensor_tensor(SQ[:, 0:GLA_W], O[:, i, :], O[:, i, :], ALU.mult))
                            link(v.tensor_reduce(hs[:, i * GLA_HEADS:(i + 1) * GLA_HEADS],
                                                 SQ[:, 0:GLA_W].rearrange("p (h c) -> p h c", h=GLA_HEADS), AX_X, ALU.add))

                        for i in range(HT_):
                            dve.wait_ge(scores, i + 1)
                            if i:
                                dve.wait_ge(o_done, i)
                            for b in range(2):
                                v.copy_predicated(out=PT[:].rearrange("p (a b) c -> p b a c", b=2)[:, b], mask=causal2,
                                                  data=banks[6 + b][:, 0:2 * P].rearrange("p (a c) -> p a c", c=P)
                                                  ).then_inc(bank_read[6 + b], 1)
                            if i:
                                head_squares(i - 1)
                            dve.wait_ge(kv_done, i + 1)
                            for c in range(2):
                                n = 2 * i + c
                                for pr in range(2):
                                    ins = v.scalar_tensor_tensor(
                                        out=state[:, n + 1, pr, :], in0=state[:, n, pr, :],
                                        scalar=E1[:, pr, (n + 1) * CHUNK - 1:(n + 1) * CHUNK],
                                        in1=banks[6 + c][:, pr * DV:(pr + 1) * DV], op0=ALU.mult, op1=ALU.add)
                                    if pr == 0:
                                        link(ins)
                                ins.then_inc(bank_read[6 + c], 1)
                                mixer_read(dve, 6 + c, f"kv{i}")
                        head_squares(HT_ - 1)
                        v.tensor_scalar(hs[:], hs[:], 1.0 / DV, EPS, ALU.mult, ALU.add).then_inc(head_ms, 1)
                        link(v.tensor_copy(state[:, 0], state[:, NCH]))
                        for i in range(HT_):
                            tile_read(dve, "vg", i)
                        link(v.tensor_tensor(SQ[:], flat(VG), flat(VG), ALU.mult))
                        link(v.tensor_reduce(gs[:], SQ[:].rearrange("p (h c) -> p h c", c=GM_DH), AX_X, ALU.add))
                        v.tensor_scalar(gs[:], gs[:], 1.0 / GM_DH, EPS, ALU.mult, ALU.add).then_inc(vg_ms, 1)
                        dve.wait_ge(head_rstd, 1)
                        for i in range(HT_):
                            oh = O[:, i, :].rearrange("p (h c) -> p h c", h=GLA_HEADS)
                            link(v.tensor_tensor(oh, oh, hr[:, i * GLA_HEADS:(i + 1) * GLA_HEADS].unsqueeze(2)
                                                 .broadcast_to([P, GLA_HEADS, DV]), ALU.mult))
                            tile_read(dve, "g", i)
                            v.tensor_tensor(O[:, i, :], O[:, i, :], GG[:, i, :], ALU.mult).then_inc(og_ready, 1)

                        def conv(f):
                            tb, tc = first_tile[f"conv{f}"] + 1, first_tile[f"conv{f}"] + 2
                            link(v.tensor_copy(Hc[:, 0:CONV_K - 1], halo[:, f, :]))
                            tile_read(dve, f"conv{f}", 0)
                            tile_done(dve, f"conv{f}", 2)
                            v.tensor_tensor(Hc[:, CONV_K - 1:], bank_of(tc)[:], SQ[:, 0:HTOK], ALU.mult
                                            ).then_inc(bank_read[tc % RING], 1)
                            tile_read(dve, f"conv{f}", 2)
                            link(v.tensor_scalar(Z[:, f, :], Hc[:, 0:HTOK], cw[:, f, 0:1], None, ALU.mult))
                            for tap in range(1, CONV_K):
                                link(v.scalar_tensor_tensor(out=Z[:, f, :], in0=Hc[:, tap:tap + HTOK],
                                                            scalar=cw[:, f, tap:tap + 1], in1=Z[:, f, :],
                                                            op0=ALU.mult, op1=ALU.add))
                            v.tensor_tensor(Z[:, f, :], bank_of(tb)[:], Z[:, f, :], ALU.mult
                                            ).then_inc(bank_read[tb % RING], 1)
                            link(v.tensor_copy(halo[:, f, :], Hc[:, HTOK:]))
                            dve.wait_ge(m_hi_ready, 1 + (GLA_HEADS + 1) * f)
                            v.tensor_tensor(mT_lo[:, 6 + f, :], Z[:, f, :], mT_hi[:, 6 + f, :].bitcast(F32),
                                            ALU.subtract).then_inc(conv_split, 1)

                        dve.wait_ge(param["conv"], 16)
                        dve.wait_ge(kd_tr, 2)
                        conv(0)
                        dve.wait_ge(param["gla"], 16)
                        for h in range(GLA_HEADS):
                            dve.wait_ge(m_hi_ready, 1 + h + 1)
                            v.scalar_tensor_tensor(out=mT_lo[:, h, :], in0=banks[6 + h % 2][:], scalar=gla_gain[:],
                                                   in1=mT_hi[:, h, :].bitcast(F32), op0=ALU.mult, op1=ALU.subtract
                                                   ).then_inc(bank_read[6 + h % 2], 1)
                        dve.wait_ge(vg_rstd, 1)
                        dve.wait_ge(param["gm"], 16)
                        vh = VG[:].rearrange("p i (h c) -> p (i h) c", c=GM_DH)
                        link(v.tensor_tensor(vh, vh, gr[:].unsqueeze(2).broadcast_to([P, HT_ * GM_HEADS, GM_DH]), ALU.mult))
                        v.tensor_tensor(VG[:], VG[:], gm_gain[:].unsqueeze(1).broadcast_to([P, HT_, GM_W]), ALU.mult
                                        ).then_inc(vg_normed, 1)
                        dve.wait_ge(param["spb"], 16)
                        for b in range(2):
                            dve.wait_ge(mixed, b + 1)
                            tmp = K[:, b, :]
                            link(v.tensor_tensor(tmp.rearrange("p (i h c) -> p i h c", i=2, h=GM_HEADS),
                                                 banks[6 + b][:].rearrange("p (i h c) -> p i h c", i=2, h=GM_HEADS),
                                                 sp_bias[:].unsqueeze(1).unsqueeze(3)
                                                 .broadcast_to([P, 2, GM_HEADS, GM_DH]), ALU.add))
                            v.tensor_tensor(U[:, 2 * b:2 * b + 2, :].rearrange("p i c -> p (i c)"),
                                            U[:, 2 * b:2 * b + 2, :].rearrange("p i c -> p (i c)"), tmp, ALU.mult
                                            ).then_inc(bank_read[6 + b], 1)
                        conv(1)
                        for f in range(2):
                            dve.wait_ge(m_hi_ready, GLA_HEADS + 2 + f + 1)
                            v.tensor_tensor(mT_lo[:, 4 + f, :], banks[6 + f][:], mT_hi[:, 4 + f, :].bitcast(F32),
                                            ALU.subtract).then_inc(bank_read[6 + f], 1)
                        for g in range(2):
                            for i in range(HT_):
                                t = first_tile[f"out{g}"] + i
                                tile_done(dve, f"out{g}", i)
                                xs = X[:, bass.ds(half * HT_ + i, 1), g * BANK:(g + 1) * BANK].rearrange("p a d -> p (a d)")
                                v.tensor_tensor(xs, xs, bank_of(t)[:], ALU.add).then_inc(bank_read[t % RING], 1)

                phase(sems, mixer)

        LK = KT // 2

        def moe(L):
            with ExitStack() as ctx:
                R_gu = [sb(f"R_gu{s}", [P, 2, KT, DX], F32, ctx) for s in range(2)]
                R_dn = [sb(f"R_dn{s}", [P, DX // P, D], F32, ctx) for s in range(2)]
                XB = [sb(f"XB{s}", [P, D], F32, ctx) for s in range(2)]
                gu_loaded = [[ctx.enter_context(nc.semaphore(f"gu_loaded{s}_{h}")) for h in range(2)] for s in range(2)]
                dn_loaded = [ctx.enter_context(nc.semaphore(f"dn_loaded{s}")) for s in range(2)]
                weight_sems = gu_loaded[0] + gu_loaded[1] + dn_loaded

                def load_gu(sp, s, e, wait=None):
                    for h in range(2):
                        if wait:
                            wait(h)
                        for m, w in enumerate((w_gate, w_up)):
                            sp.dma_start(R_gu[s][:, m, h * LK:(h + 1) * LK],
                                         w.rearrange("l e (p k) f -> (l e) p k f", k=KT)
                                         [bass.ds(e, 1), :, h * LK:(h + 1) * LK].rearrange("a p k f -> (a p) k f")
                                         ).then_inc(gu_loaded[s][h], 16)

                def load_dn(sp, s, e):
                    sp.dma_start(R_dn[s][:], w_down.rearrange("l e (p m) d -> (l e) p m d", m=DX // P)
                                 [bass.ds(e, 1)].rearrange("a p m d -> (a p) m d")).then_inc(dn_loaded[s], 16)

                route(L, load_gu, load_dn, XB)
                experts(L, weight_sems, gu_loaded, dn_loaded, load_gu, load_dn, R_gu, R_dn, XB)

        def expert_of(sp, L, column):
            return sp.snap(sp.value_load(blk_exp[0:1, column], min_val=0, max_val=N_EXP - 1) + L * N_EXP)

        def route(L, load_gu, load_dn, XB):
            with ExitStack() as ctx:
                local = lambda name, shape, dt=F32: sb(name, shape, dt, ctx)
                NLOG = N_GROUPS + N_EXP
                NQ = NT * TOP_K
                BIG = 64.0
                gain = local("ffn_gain", [P, D])
                gain_col = local("ffn_gain_col", [P, KT])
                w_rt = local("w_rt", [P, KT, NLOG])
                w_rg = local("w_rg", [P, KT, NLOG])
                b_rt = local("b_rt", [P, NLOG])
                sq = local("sq", [P, D])
                ss = local("ss8", [P, NT])
                rs = local("rs8", [P, NT])
                Hr = local("Hr", [P, NT, D])
                XT = local("XT", [P, KT, SEQ])
                LT = local("LT", [NLOG, SEQ])
                LG = local("LG", [P, NT, NLOG])
                m1 = local("m1", [P, NT, 1])
                m2 = local("m2", [P, NT, 1])
                eq4 = local("eq4", [P, NT, N_GROUPS])
                eq8 = local("eq8", [P, NT, PER_GROUP])
                EIN = local("EIN", [P, NT, PER_GROUP])
                E2nd = local("E2nd", [P, NT, PER_GROUP])
                g_id = local("g_id", [P, NT, 1])
                e_id = local("e_id", [P, NT, TOP_K])
                g_ex = local("g_ex", [P, NT, N_GROUPS])
                g_w = local("g_w", [P, NT])
                hot4 = local("hot4", [P, NT, N_GROUPS])
                hot8 = local("hot8", [P, NT, PER_GROUP])
                pick = local("pick", [P, NT, PER_GROUP, N_GROUPS])
                e_dif = local("e_dif", [P, NT, 1])
                M = local("M", [P, NT, TOP_K, N_EXP])
                MS = local("MS", [P, NT + 1, N_EXP], BF16)
                cnt_i = local("cnt_i", [P, N_EXP], I32)
                nb = local("nb", [P, N_EXP])
                nb_end = local("nb_end", [P, N_EXP])
                base = local("base", [P, N_EXP])
                rank = local("rank", [P, NT, N_EXP])
                MR = local("MR", [P, NT, TOP_K, N_EXP])
                dest = local("dest", [P, NQ])
                dest_i = local("dest_i", [P, NQ], I32)
                low_i = local("low_i", [P, NQ], I32)
                low = local("low", [P, NQ], BF16)
                high = local("high", [P, NQ], BF16)
                be_col = local("be_col", [P, 1])
                hot_p = local("hot_p", [P, NQ, P], BF16)
                hot_b = local("hot_b", [P, NQ, NCOL], BF16)
                hot_v = local("hot_v", [P, NQ, 2, NCOL], BF16)
                row1 = local("row1", [P, NCOL])
                row_f = local("row_f", [P, NCOL])
                hole = local("hole", [P, NCOL])
                np_i = local("np_i", [P, 1], I32)
                before_b = local("before_b", [P, P], BF16)
                ones_b = local("ones_b", [P, P], BF16)
                iota_b = local("iota_b", [P, P], BF16)
                iota_i = local("iota_i", [P, PER_GROUP])
                iota_e = local("iota_e", [P, N_EXP])

                sems = []

                def sem(name):
                    sems.append(ctx.enter_context(nc.semaphore(name)))
                    return sems[-1]

                gain_loaded, router_loaded, rows_stored = sem("ffn_gain_loaded"), sem("router_loaded"), sem("rows_stored")
                sumsq, rstd_in, rstd_ready = sem("sumsq8"), sem("rstd_in8"), sem("rstd_ready8")
                x_tr, xT_act, xT_dve, w_ready = sem("x_tr8"), sem("xT_act8"), sem("xT_dve8"), sem("router_scaled")
                logits, logits_out, logits_tr = sem("logits"), sem("logits_out"), sem("logits_transposed")
                row_dve, row_scaled, row_pool, dve_step = (sem(n) for n in ("row_dve", "row_scaled", "row_pool", "dve_step8"))
                hot_b_ready, hot_q_ready, xb_zero = sem("hot_b_ready"), sem("hot_q_ready"), sem("xb_zeroed")
                g_dif_ready, g_exp_ready = sem("g_dif_ready"), sem("g_exp_ready")
                e_dif_ready, e_exp_ready = sem("e_dif_ready"), sem("e_exp_ready")
                ms_ready, ranked, be_ready, be_row = sem("ms_ready"), sem("ranked"), sem("be_ready"), sem("be_row")
                hot_ready, tabled, blk_ready = sem("hot_ready"), sem("tabled"), sem("blk_ready")

                pairs = ((banks[0], banks[1]), (banks[2], banks[3]), (banks[6], banks[7]))
                bk_log, bk_back, bk_rank, bk_be, bk_slot = (banks[4], banks[5]), banks[6], banks[7], banks[1], banks[0]
                HK = KT // 2
                ON_DVE = NT // 2
                ROWS_DVE = NT - 3

                def copied(eng, j):
                    eng.wait_ge(xT_dve, 2 * (j + 1) if j < ON_DVE else 2 * ON_DVE + j + 1 - ON_DVE)
                    if j >= ON_DVE:
                        eng.wait_ge(xT_act, j + 1 - ON_DVE)

                def xT_part(j, b):
                    return (XT[:, b * HK:(b + 1) * HK, j * P:(j + 1) * P],
                            pairs[j % 3][b][:].rearrange("p (k c) -> p k c", k=HK))

                def program(block):
                    @block.sync
                    def _(sp):
                        for at, w in ((slice(0, N_GROUPS), w_router_group), (slice(N_GROUPS, NLOG), w_router_expert)):
                            sp.dma_start(w_rt[:, :, at], w[bass.ds(L, 1)].rearrange("a p k g -> (a p) k g")
                                         ).then_inc(router_loaded, 16)
                        sp.dma_start(gain_col[:], ffn_norm_col[bass.ds(L, 1)].rearrange("a p k -> (a p) k")
                                     ).then_inc(router_loaded, 16)
                        for at, w in ((slice(0, N_GROUPS), b_router_group), (slice(N_GROUPS, NLOG), b_router_expert)):
                            sp.dma_start(b_rt[:, at], w[bass.ds(L, 1), :].broadcast_to([P, at.stop - at.start])
                                         ).then_inc(router_loaded, 16)
                        sp.dma_start(gain[:], ffn_norm[bass.ds(L, 1), :].broadcast_to([P, D])).then_inc(gain_loaded, 16)
                        first = sp.snap(L * N_EXP)
                        load_gu(sp, 0, first)
                        load_dn(sp, 0, first)
                        for j in range(NT):
                            if j < ROWS_DVE:
                                sp.wait_ge(row_dve, j + 1)
                            else:
                                sp.wait_ge(row_pool, j - ROWS_DVE + 1)
                            sp.dma_start(h_dram[j * P:(j + 1) * P, :], Hr[:, j, :]).then_inc(rows_stored, 16)
                        sp.wait_ge(blk_ready, 1)
                        load_gu(sp, 1, expert_of(sp, L, slice(1, 2)))
                        sp.wait_ge(rows_stored, 16 * NT)

                    @block.gpsimd
                    def _(pool):
                        g = nc.gpsimd
                        for s in range(2):
                            g.memset(XB[s][:], 0.0).then_inc(xb_zero, 1)
                        pool.wait_ge(rstd_in, 1)
                        g.tensor_tensor(rs[:], ss[:], minus_half[:, 0:NT], ALU.pow).then_inc(rstd_ready, 1)
                        pool.wait_ge(gain_loaded, 16)
                        for j in range(ROWS_DVE, NT):
                            pool.wait_ge(row_scaled, j - ROWS_DVE + 1)
                            g.tensor_tensor(Hr[:, j, :], Hr[:, j, :], gain[:], ALU.mult).then_inc(row_pool, 1)
                        pool.wait_ge(hot_b_ready, 1)
                        g.tensor_tensor(hot_v[:, :, 1, :], hot_b[:], q_map[:].rearrange("p j k -> p (j k)").unsqueeze(2)
                                        .broadcast_to([P, NQ, NCOL]), ALU.mult).then_inc(hot_q_ready, 1)

                    @block.scalar
                    def _(act):
                        a = nc.scalar.activation
                        for j in range(NT):
                            if j:
                                act.wait_ge(sumsq, j)
                            a(sq[:], X[:, j, :], ACT.Square, accum_out=ss[:, j:j + 1]).then_inc(sumsq, 1)
                        for j in range(ON_DVE, NT):
                            act.wait_ge(x_tr, j + 1)
                            dst, src = xT_part(j, 0)
                            a(dst, src, ACT.Copy).then_inc(xT_act, 1)
                        act.wait_ge(rstd_ready, 1)
                        for j in range(ROWS_DVE, NT):
                            a(Hr[:, j, :], X[:, j, :], ACT.Copy, scale=rs[:, j:j + 1]).then_inc(row_scaled, 1)
                        for h in range(HALVES):
                            act.wait_ge(logits, h + 1)
                            a(LT[:, h * BANK:(h + 1) * BANK], bk_log[h][0:NLOG, :], ACT.Copy).then_inc(logits_out, 1)
                        act.wait_ge(g_dif_ready, 1)
                        a(g_ex[:], hot4[:], ACT.Exp).then_inc(g_exp_ready, 1)
                        act.wait_ge(e_dif_ready, 1)
                        a(e_dif[:], e_dif[:], ACT.Exp).then_inc(e_exp_ready, 1)

                    @block.tensor
                    def _(pe):
                        mm, tr = nc.tensor.matmul, nc.tensor.transpose

                        def x_transpose(j):
                            if j >= 3:
                                copied(pe, j - 3)
                            for k in range(KT):
                                ins = tr(pairs[j % 3][k // HK][:, (k % HK) * P:(k % HK + 1) * P],
                                         X[:, j, k * P:(k + 1) * P], ident[:])
                            ins.then_inc(x_tr, 1)

                        def logits_of(h, ks=range(KT)):
                            copied(pe, (h + 1) * HT_ - 1)
                            for k in ks:
                                ins = mm(bk_log[h][0:NLOG, :], w_rg[:, k, :], XT[:, k, h * BANK:(h + 1) * BANK],
                                         start=(k == 0), stop=(k == KT - 1))
                            if k == KT - 1:
                                ins.then_inc(logits, 1)

                        for j in range(NT - 1):
                            x_transpose(j)
                        pe.wait_ge(w_ready, 1)
                        logits_of(0, range(KT // 2))
                        x_transpose(NT - 1)
                        logits_of(0, range(KT // 2, KT))
                        logits_of(1)
                        for j in range(NT):
                            if j % HT_ == 0:
                                pe.wait_ge(logits_out, j // HT_ + 1)
                            ins = tr(bk_back[:, j * NLOG:(j + 1) * NLOG], LT[:, j * P:(j + 1) * P],
                                     ident[0:NLOG, 0:NLOG])
                        ins.then_inc(logits_tr, 1)
                        pe.wait_ge(ms_ready, 1)
                        mm(bk_rank[:, 0:(NT + 1) * N_EXP], before_b[:], MS[:].rearrange("p j e -> p (j e)"),
                           start=True, stop=False)
                        for j in range(NT):
                            ins = mm(bk_rank[:, (j + 1) * N_EXP:(NT + 1) * N_EXP].rearrange("p (r e) -> p r e", e=N_EXP),
                                     ones_b[:], MS[:, j:j + 1, :].broadcast_to([P, NT - j, N_EXP]), start=False,
                                     stop=(j == NT - 1))
                        ins.then_inc(ranked, 1)
                        pe.wait_ge(be_ready, 1)
                        mm(bk_be[0:1, 0:NCOL], be_col[:], ident[:, 0:NCOL], start=True, stop=True).then_inc(be_row, 1)
                        pe.wait_ge(hot_q_ready, 1)
                        for q in range(NQ):
                            if q % (NQ // 2) == 0:
                                pe.wait_ge(hot_ready, q // (NQ // 2) + 1)
                            ins = mm(bk_slot[:, 0:2 * NCOL], hot_p[:, q, :], hot_v[:, q].rearrange("p v b -> p (v b)"),
                                     start=(q == 0), stop=(q == NQ - 1))
                        ins.then_inc(tabled, 1)

                    @block.vector
                    def _(dve):
                        link = chain(dve, dve_step)
                        v = nc.vector
                        link(v.tensor_copy(before_b[:], before[:]))
                        link(v.tensor_copy(ones_b[:], ones[:]))
                        link(v.tensor_copy(iota_b[:], iota_row[:]))
                        link(v.tensor_scalar(iota_i[:], iota_row[:, 0:PER_GROUP], -BIG, None, ALU.add))
                        link(v.tensor_scalar(iota_e[:], iota_row[:, 0:N_EXP], -BIG * (PER_GROUP + 1), None, ALU.add))
                        link(v.memset(MS[:, NT, :], 0.0))
                        for j in range(NT):
                            dve.wait_ge(x_tr, j + 1)
                            for b in range(2):
                                if j < ON_DVE or b == 1:
                                    dst, src = xT_part(j, b)
                                    v.tensor_copy(dst, src).then_inc(xT_dve, 1)
                            if j == NT - 2:
                                dve.wait_ge(sumsq, NT)
                                v.tensor_scalar(ss[:], ss[:], 1.0 / D, EPS, ALU.mult, ALU.add).then_inc(rstd_in, 1)
                            if j == 2:
                                dve.wait_ge(router_loaded, 80)
                                v.tensor_tensor(w_rg[:], w_rt[:], gain_col[:].unsqueeze(2).broadcast_to([P, KT, NLOG]),
                                                ALU.mult).then_inc(w_ready, 1)
                        dve.wait_ge(rstd_ready, 1)
                        dve.wait_ge(gain_loaded, 16)
                        for j in range(ROWS_DVE):
                            v.scalar_tensor_tensor(out=Hr[:, j, :], in0=X[:, j, :], scalar=rs[:, j:j + 1],
                                                   in1=gain[:], op0=ALU.mult, op1=ALU.mult).then_inc(row_dve, 1)
                        dve.wait_ge(logits_tr, 1)
                        link(v.tensor_tensor(LG[:], bk_back[:, 0:NT * NLOG].rearrange("p (j e) -> p j e", e=NLOG),
                                             rs[:].unsqueeze(2).broadcast_to([P, NT, NLOG]), ALU.mult))
                        link(v.tensor_tensor(LG[:], LG[:], b_rt[:].unsqueeze(1).broadcast_to([P, NT, NLOG]), ALU.add))

                        def index_of(out_id, values, top, eq, n):
                            link(v.tensor_tensor(eq[:], values, top.broadcast_to([P, NT, n]), ALU.is_equal))
                            link(v.tensor_tensor(eq[:], eq[:], iota_i[:, 0:n].unsqueeze(1).broadcast_to([P, NT, n]),
                                                 ALU.mult))
                            link(v.tensor_reduce(out_id, eq[:], AX_X, ALU.min))

                        groups = LG[:, :, 0:N_GROUPS]
                        link(v.tensor_reduce(m1[:, :, 0], groups, AX_X, ALU.max))
                        v.tensor_tensor(hot4[:], groups, m1[:].broadcast_to([P, NT, N_GROUPS]), ALU.subtract
                                        ).then_inc(g_dif_ready, 1)
                        index_of(g_id[:, :, 0], groups, m1[:], eq4, N_GROUPS)
                        dve.wait_ge(g_exp_ready, 1)
                        link(v.tensor_tensor(hot4[:], iota_i[:, 0:N_GROUPS].unsqueeze(1).broadcast_to([P, NT, N_GROUPS]),
                                             g_id[:].broadcast_to([P, NT, N_GROUPS]), ALU.is_equal))
                        link(v.tensor_tensor(pick[:],
                                             LG[:, :, N_GROUPS:].rearrange("p j (g e) -> p j e g", g=N_GROUPS),
                                             hot4[:].unsqueeze(2).broadcast_to([P, NT, PER_GROUP, N_GROUPS]), ALU.mult))
                        link(v.tensor_reduce(EIN[:], pick[:], AX_X, ALU.add))
                        link(v.tensor_reduce(m1[:, :, 0], EIN[:], AX_X, ALU.max))
                        index_of(e_id[:, :, 0], EIN[:], m1[:], eq8, PER_GROUP)
                        link(v.tensor_tensor(hot8[:], iota_i[:].unsqueeze(1).broadcast_to([P, NT, PER_GROUP]),
                                             e_id[:, :, 0:1].broadcast_to([P, NT, PER_GROUP]), ALU.is_equal))
                        link(v.scalar_tensor_tensor(out=E2nd[:], in0=hot8[:], scalar=-3.0e38, in1=EIN[:], op0=ALU.mult,
                                                    op1=ALU.add))
                        link(v.tensor_reduce(m2[:, :, 0], E2nd[:], AX_X, ALU.max))
                        v.tensor_tensor(e_dif[:], m2[:], m1[:], ALU.subtract).then_inc(e_dif_ready, 1)
                        index_of(e_id[:, :, 1], E2nd[:], m2[:], eq8, PER_GROUP)
                        link(v.scalar_tensor_tensor(out=e_id[:], in0=g_id[:].broadcast_to([P, NT, TOP_K]),
                                                    scalar=float(PER_GROUP), in1=e_id[:], op0=ALU.mult, op1=ALU.add))
                        link(v.tensor_tensor(M[:].rearrange("p j k e -> p (j k) e"),
                                             iota_e[:].unsqueeze(1).broadcast_to([P, NQ, N_EXP]),
                                             e_id[:].rearrange("p j k -> p (j k)").unsqueeze(2)
                                             .broadcast_to([P, NQ, N_EXP]), ALU.is_equal))
                        v.tensor_tensor(MS[:, 0:NT, :], M[:, :, 0, :], M[:, :, 1, :], ALU.add).then_inc(ms_ready, 1)
                        link(v.tensor_reduce(g_w[:], g_ex[:], AX_X, ALU.add))
                        link(v.reciprocal(g_w[:], g_w[:]))
                        dve.wait_ge(e_exp_ready, 1)
                        Wt = lambda k: Wtok[:, :, k:k + 1]
                        link(v.tensor_scalar(Wt(0), e_dif[:], 1.0, None, ALU.add))
                        link(v.reciprocal(Wt(0), Wt(0)))
                        link(v.tensor_tensor(Wt(0), Wt(0), g_w[:].unsqueeze(2), ALU.mult))
                        link(v.tensor_tensor(Wt(1), Wt(0), e_dif[:], ALU.mult))
                        dve.wait_ge(ranked, 1)
                        link(v.tensor_scalar(cnt_i[:], bk_rank[:, NT * N_EXP:(NT + 1) * N_EXP], float(P - 1), None,
                                             ALU.add))
                        link(v.tensor_scalar(cnt_i[:], cnt_i[:], P.bit_length() - 1, None, ALU.arith_shift_right))
                        link(v.tensor_scalar(nb[:], cnt_i[:], 1.0, None, ALU.max))
                        link(v.tensor_tensor_scan(nb_end[:], ones[:, 0:N_EXP], nb[:], 0.0, ALU.mult, ALU.add))
                        link(v.tensor_scalar(base[:], nb_end[:], tok1[:], None, ALU.is_lt))
                        link(v.tensor_reduce(be_col[:], base[:], AX_X, ALU.add))
                        v.tensor_scalar(be_col[:], be_col[:], float(N_EXP - 1), None, ALU.min).then_inc(be_ready, 1)
                        link(v.tensor_tensor(base[:], nb_end[:], nb[:], ALU.subtract))
                        link(v.tensor_scalar(np_i[:], nb_end[:, N_EXP - 1:N_EXP], -1.0, None, ALU.add))
                        link(v.tensor_scalar(last_pair[:], np_i[:], 1, None, ALU.arith_shift_right))
                        dve.wait_ge(be_row, 1)
                        v.tensor_copy(blk_exp[:], bk_be[0:1, 0:NCOL]).then_inc(blk_ready, 1)
                        link(v.scalar_tensor_tensor(out=rank[:], in0=base[:].unsqueeze(1).broadcast_to([P, NT, N_EXP]),
                                                    scalar=float(P), in1=bk_rank[:, 0:NT * N_EXP]
                                                    .rearrange("p (j e) -> p j e", e=N_EXP), op0=ALU.mult, op1=ALU.add))
                        link(v.tensor_tensor(MR[:], M[:], rank[:].unsqueeze(2).broadcast_to([P, NT, TOP_K, N_EXP]),
                                             ALU.mult))
                        link(v.tensor_reduce(dest[:], MR[:].rearrange("p j k e -> p (j k) e"), AX_X, ALU.add))
                        link(v.tensor_copy(dest_i[:], dest[:]))
                        link(v.tensor_scalar(low_i[:], dest_i[:], P - 1, None, ALU.bitwise_and))
                        link(v.tensor_scalar(dest_i[:], dest_i[:], P.bit_length() - 1, None, ALU.arith_shift_right))
                        link(v.tensor_copy(low[:], low_i[:]))
                        link(v.tensor_copy(high[:], dest_i[:]))
                        v.tensor_tensor(hot_b[:], iota_b[:, 0:NCOL].unsqueeze(1).broadcast_to([P, NQ, NCOL]),
                                        high[:].unsqueeze(2).broadcast_to([P, NQ, NCOL]), ALU.is_equal
                                        ).then_inc(hot_b_ready, 1)
                        dve.wait_ge(hot_b_ready, 1)
                        v.tensor_scalar(hot_v[:, :, 0, :], hot_b[:], tok1[:], None, ALU.mult)
                        for h in range(2):
                            at = slice(h * NQ // 2, (h + 1) * NQ // 2)
                            v.tensor_tensor(hot_p[:, at], iota_b[:].unsqueeze(1).broadcast_to([P, NQ // 2, P]),
                                            low[:, at].unsqueeze(2).broadcast_to([P, NQ // 2, P]), ALU.is_equal
                                            ).then_inc(hot_ready, 1)
                        dve.wait_ge(tabled, 1)
                        link(v.tensor_scalar(hole[:], bk_slot[:, 0:NCOL], 0.0, EMPTY, ALU.is_equal, ALU.mult))
                        link(v.scalar_tensor_tensor(out=row1[:], in0=bk_slot[:, 0:NCOL], scalar=-1.0, in1=hole[:],
                                                    op0=ALU.add, op1=ALU.add))
                        link(v.scalar_tensor_tensor(out=row_f[:], in0=bk_slot[:, NCOL:2 * NCOL], scalar=float(P),
                                                    in1=row1[:], op0=ALU.mult, op1=ALU.add))
                        link(v.tensor_copy(slot_row[:], row_f[:]))
                        link(v.tensor_scalar(hole[:], row_f[:], float(SEQ), -float(SEQ), ALU.is_ge, ALU.mult))
                        link(v.tensor_tensor(slot_tok[:], row_f[:], hole[:], ALU.add))

                phase(sems, program)

        def experts(L, weight_sems, gu_loaded, dn_loaded, load_gu, load_dn, R_gu, R_dn, XB):
            with ExitStack() as ctx:
                local = lambda name, shape, dt=F32: sb(name, shape, dt, ctx)
                KU = 2
                GU_UNITS, DM = KT // KU, DX // P
                UNITS = GU_UNITS + DM
                ON_POOL = GU_UNITS - 1
                gu_hi, gu_lo = ([local(f"{n}{s}", [P, KT, 2 * DX], F32R) for s in range(2)] for n in ("gu_hi", "gu_lo"))
                dn_hi, dn_lo = (local(n, [P, DM, D], F32R) for n in ("dn_hi", "dn_lo"))
                xT_hi = local("xT_hi", [P, KT, P], F32R)
                xT_lo = local("xT_lo", [P, KT, P], F32R)
                SG = local("SG", [P, DX])
                HB = local("HB", [P, DX])
                hbT_hi = local("hbT_hi", [P, DM, P], F32R)
                hbT_lo = local("hbT_lo", [P, DM, P], F32R)
                YB = [local(f"YB{s}", [P, D]) for s in range(2)]
                spare = local("spare", [P, 1])
                idx_in = [local(f"idx_in{s}", [P, 1], I32) for s in range(2)]
                idx_out = [local(f"idx_out{s}", [P, 1], I32) for s in range(2)]

                sems = []

                def sem(name):
                    sems.append(ctx.enter_context(nc.semaphore(name)))
                    return sems[-1]

                two = lambda name: [sem(f"{name}{s}") for s in range(2)]
                rows_in, rows_out = two("rows_in"), two("rows_out")
                yb_free = two("yb_free")
                in_set, out_set = two("idx_in_set"), two("idx_out_set")
                unit_hi = [sem(f"unit_hi{u}") for u in range(UNITS)]
                unit_lo = [sem(f"unit_lo{u}") for u in range(UNITS)]
                unit_used = [sem(f"unit_used{u}") for u in range(UNITS)]
                x_tr, xT_hi_ready, xT_lo_ready = sem("x_transposed"), two("xT_hi_ready"), two("xT_lo_ready")
                sg_ready, hb_ready, h_tr = sem("sg_ready"), sem("hb_ready"), sem("h_transposed")
                hbT_hi_ready, hbT_lo_ready = sem("hbT_hi_ready"), sem("hbT_lo_ready")
                y_act, y_dve = sem("y_act"), sem("y_dve")
                pool_turn, table_set = sem("pool_turn"), sem("table_set")

                bk_x, bk_gu, bk_h, bk_y = (banks[0], banks[1]), (banks[2], banks[3]), banks[4], (banks[5], banks[6])
                HK = KT // 2

                def unit(u, s):
                    if u < GU_UNITS:
                        ks = slice(u * KU, (u + 1) * KU)
                        parts = [w[:, ks, :].rearrange("p k (m f) -> p k m f", m=2) for w in (gu_hi[s], gu_lo[s])]
                        return [R_gu[s][:, :, ks, :].rearrange("p m k f -> p k m f")] + parts
                    m = u - GU_UNITS
                    return [R_dn[s][:, m, :], dn_hi[:, m, :], dn_lo[:, m, :]]

                def over_blocks(eng, body):
                    last = eng.snap(eng.value_load(last_pair[0:1, 0:1], min_val=ASSIGN // P // 2 - 1,
                                                   max_val=NBLK // 2 - 1))
                    with eng.Fori(0, last) as i:
                        body(i, 0, True, True)
                        body(i, 1, True, True)
                    body(last, 0, True, False)
                    body(last, 1, False, False)
                    return last

                def program(block):
                    @block.sync
                    def _(sp):
                        def body(i, s, next_ahead, second_ahead):
                            b = 2 * i + s

                            def split(h):
                                for u in range(h * LK // KU, (h + 1) * LK // KU):
                                    sp.wait_ge(unit_lo[u], b + 3)

                            if second_ahead:
                                load_gu(sp, s, expert_of(sp, L, bass.ds(b + 2, 1)), split)
                            if next_ahead:
                                e_dn = expert_of(sp, L, bass.ds(b + 1, 1))
                                for u in range(GU_UNITS, UNITS):
                                    sp.wait_ge(unit_lo[u], b + 2)
                                load_dn(sp, 1 - s, e_dn)

                        over_blocks(sp, body)

                    @block.gpsimd
                    def _(pool):
                        g = nc.gpsimd
                        last_row, last_assign = g.to_reg(SEQ - 1), g.to_reg(ASSIGN - 1)

                        def gather(s):
                            g.indirect_dma_start(out=XB[s][:], out_offset=None, in_=h_dram[:, :],
                                                 in_offset=bass.IndirectOffsetOnAxis(ap=idx_in[s][:, 0:1], axis=0),
                                                 bounds_check=last_row, oob_is_err=False).then_inc(rows_in[s], 16)

                        def ahead(s, nth, nth_in_slot):
                            raw, hi, lo = unit(ON_POOL, s)
                            pool.wait_ge(unit_hi[ON_POOL], nth)
                            g.tensor_tensor(lo, raw, hi.bitcast(F32), ALU.subtract).then_inc(unit_lo[ON_POOL], 1)
                            pool.wait_ge(x_tr, nth)
                            pool.wait_ge(in_set[s], nth_in_slot + 1)
                            pool.sem_inc(pool_turn, 1)
                            gather(s)

                        for s in range(2):
                            pool.wait_ge(in_set[s], 1)
                            gather(s)
                        for s in range(2):
                            ahead(s, s + 1, 1)

                        def body(i, s, next_ahead, second_ahead):
                            b = 2 * i + s
                            if second_ahead:
                                ahead(s, b + 3, i + 2)
                            pool.wait_ge(out_set[s], i + 1)
                            pool.wait_ge(y_act, b + 2)
                            pool.wait_ge(y_dve, b + 2)
                            pool.sem_inc(pool_turn, 1)
                            g.indirect_dma_start(out=y_dram[:, :],
                                                 out_offset=bass.IndirectOffsetOnAxis(ap=idx_out[s][:, 0:1], axis=0),
                                                 in_=YB[s][:], in_offset=None, bounds_check=last_assign,
                                                 oob_is_err=False).then_inc(rows_out[s], 16)
                            pool.wait_ge(rows_out[s], 16 * (i + 1))
                            pool.sem_inc(yb_free[s], 1)

                        last = over_blocks(pool, body)
                        for s in range(2):
                            pool.wait_ge(rows_in[s], 16 * (last + 2))
                            pool.sem_inc(pool_turn, 1)
                        pool.dma_reset(range(rows_in[0].num, rows_out[1].num + 1))

                    @block.scalar
                    def _(act):
                        a = nc.scalar.activation

                        def high(u, s, nth_in_slot, nth):
                            raw, hi, lo = unit(u, s)
                            if u < GU_UNITS:
                                act.wait_ge(gu_loaded[s][u * KU // LK], 32 * nth_in_slot)
                            else:
                                act.wait_ge(dn_loaded[s], 16 * nth_in_slot)
                            act.wait_ge(unit_used[u], nth)
                            a(hi, raw, ACT.Copy).then_inc(unit_hi[u], 1)

                        def xT_high(nth):
                            act.wait_ge(x_tr, nth)
                            for b in range(2):
                                a(xT_hi[:, b * HK:(b + 1) * HK, :].rearrange("p k c -> p (k c)"), bk_x[b][:], ACT.Copy
                                  ).then_inc(xT_hi_ready[b], 1)

                        def silu(s, nth):
                            act.wait_ge(unit_used[GU_UNITS - 1], nth + 2)
                            act.wait_ge(hb_ready, nth)
                            a(SG[:], bk_gu[s][:, 0:DX], ACT.Silu).then_inc(sg_ready, 1)

                        act.wait_ge(table_set, 1)
                        for u in range(GU_UNITS):
                            high(u, 0, 1, 1)
                        xT_high(1)
                        for u in range(GU_UNITS):
                            high(u, 1, 1, 2)
                        silu(0, 1)
                        xT_high(2)

                        def body(i, s, next_ahead, second_ahead):
                            b = 2 * i + s
                            if s == 0:
                                act.wait_ge(table_set, i + 1)
                                a(spare[:], ones[:, 0:1], ACT.Silu).then_inc(table_set, 1)
                            act.wait_ge(h_tr, b + 1)
                            a(hbT_hi[:].rearrange("p m c -> p (m c)"), bk_h[:, 0:DX], ACT.Copy).then_inc(hbT_hi_ready, 1)
                            for u in range(GU_UNITS, UNITS):
                                high(u, s, i + 1, b + 1)
                            if second_ahead:
                                for u in range(GU_UNITS):
                                    high(u, s, i + 2, b + 3)
                            if next_ahead:
                                silu(1 - s, b + 2)
                            if second_ahead:
                                xT_high(b + 3)
                            act.wait_ge(unit_used[UNITS - 1], b + 2)
                            act.wait_ge(yb_free[s], i + 1)
                            a(YB[s][:, 0:BANK], bk_y[0][:], ACT.Copy).then_inc(y_act, 1)

                        over_blocks(act, body)

                    @block.vector
                    def _(dve):
                        v = nc.vector
                        for s in range(2):
                            v.tensor_copy(idx_in[s][:], slot_tok[:, s:s + 1]).then_inc(in_set[s], 1)
                        dve.sem_inc(table_set, 1)
                        dve.sem_inc(hb_ready, 1)
                        dve.sem_inc(y_act, 1)
                        dve.sem_inc(y_dve, 1)
                        for u in range(UNITS):
                            dve.sem_inc(unit_lo[u], 2)
                            dve.sem_inc(unit_used[u], 2 if u < GU_UNITS else 1)
                        for s in range(2):
                            dve.sem_inc(yb_free[s], 1)

                        def low(u, s, nth):
                            raw, hi, lo = unit(u, s)
                            dve.wait_ge(unit_hi[u], nth)
                            v.tensor_tensor(lo, raw, hi.bitcast(F32), ALU.subtract).then_inc(unit_lo[u], 1)

                        def xT_low(nth):
                            for b in range(2):
                                half = slice(b * HK, (b + 1) * HK)
                                dve.wait_ge(xT_hi_ready[b], nth)
                                v.tensor_tensor(xT_lo[:, half, :].rearrange("p k c -> p (k c)"), bk_x[b][:],
                                                xT_hi[:, half, :].rearrange("p k c -> p (k c)").bitcast(F32),
                                                ALU.subtract).then_inc(xT_lo_ready[b], 1)

                        def hidden(s, nth):
                            dve.wait_ge(sg_ready, nth)
                            v.tensor_tensor(HB[:], bk_gu[s][:, DX:2 * DX], SG[:], ALU.mult).then_inc(hb_ready, 1)

                        def next_rows(s, nth_in_slot, column):
                            dve.wait_ge(rows_in[s], 16 * nth_in_slot)
                            v.tensor_copy(idx_in[s][:], slot_tok[:, column]).then_inc(in_set[s], 1)

                        for u in range(ON_POOL):
                            low(u, 0, 1)
                        xT_low(1)
                        next_rows(0, 1, slice(2, 3))
                        next_rows(1, 1, slice(3, 4))
                        for u in range(ON_POOL):
                            low(u, 1, 2)
                        hidden(0, 1)
                        xT_low(2)

                        def body(i, s, next_ahead, second_ahead):
                            b = 2 * i + s
                            dve.wait_ge(hbT_hi_ready, b + 1)
                            v.tensor_tensor(hbT_lo[:].rearrange("p m c -> p (m c)"), bk_h[:, 0:DX],
                                            hbT_hi[:].rearrange("p m c -> p (m c)").bitcast(F32), ALU.subtract
                                            ).then_inc(hbT_lo_ready, 1)
                            for u in range(GU_UNITS, UNITS):
                                low(u, s, b + 1)
                            dve.wait_ge(yb_free[s], i + 1)
                            v.tensor_copy(idx_out[s][:], slot_row[:, bass.ds(b, 1)]).then_inc(out_set[s], 1)
                            if second_ahead:
                                next_rows(s, i + 2, bass.ds(b + 4, 1))
                                for u in range(ON_POOL):
                                    low(u, s, b + 3)
                            if next_ahead:
                                hidden(1 - s, b + 2)
                            if second_ahead:
                                xT_low(b + 3)
                            dve.wait_ge(unit_used[UNITS - 1], b + 2)
                            v.tensor_copy(YB[s][:, BANK:], bk_y[1][:]).then_inc(y_dve, 1)

                        over_blocks(dve, body)

                    @block.tensor
                    def _(pe):
                        mm, tr = nc.tensor.matmul, nc.tensor.transpose

                        def x_transpose(s, nth_in_slot):
                            pe.wait_ge(rows_in[s], 16 * nth_in_slot)
                            rows = XB[s][:].rearrange("p (c k) -> p k c", k=KT)
                            for k in range(KT):
                                ins = tr(bk_x[k // HK][:, (k % HK) * P:(k % HK + 1) * P], rows[:, k, :], ident[:])
                            ins.then_inc(x_tr, 1)

                        def gate_up(s, nth):
                            for k in range(KT):
                                if k % HK == 0:
                                    pe.wait_ge(xT_lo_ready[k // HK], nth)
                                if k % KU == 0:
                                    pe.wait_ge(unit_lo[k // KU], nth + 2)
                                first, last = k == 0, k == KT - 1
                                mm(bk_gu[s][:], xT_hi[:, k, :], gu_hi[s][:, k, :], start=first, stop=False)
                                mm(bk_gu[s][:], xT_hi[:, k, :], gu_lo[s][:, k, :], start=False, stop=False)
                                ins = mm(bk_gu[s][:], xT_lo[:, k, :], gu_hi[s][:, k, :], start=False, stop=last)
                                if k % KU == KU - 1:
                                    ins.then_inc(unit_used[k // KU], 1)

                        x_transpose(0, 1)
                        gate_up(0, 1)
                        x_transpose(1, 1)

                        def body(i, s, next_ahead, second_ahead):
                            b = 2 * i + s
                            pe.wait_ge(hb_ready, b + 2)
                            cols = HB[:].rearrange("p (c m) -> p m c", m=DM)
                            for m in range(DM):
                                ins = tr(bk_h[:, m * P:(m + 1) * P], cols[:, m, :], ident[:])
                            ins.then_inc(h_tr, 1)
                            if next_ahead:
                                gate_up(1 - s, b + 2)
                            if second_ahead:
                                x_transpose(s, i + 2)
                            pe.wait_ge(hbT_lo_ready, b + 1)
                            pe.wait_ge(y_act, b + 1)
                            pe.wait_ge(y_dve, b + 1)
                            for m in range(DM):
                                pe.wait_ge(unit_lo[GU_UNITS + m], b + 3)
                                for o in range(D // BANK):
                                    cols = slice(o * BANK, (o + 1) * BANK)
                                    first, last = m == 0, m == DM - 1
                                    mm(bk_y[o][:], hbT_hi[:, m, :], dn_hi[:, m, cols], start=first, stop=False)
                                    mm(bk_y[o][:], hbT_hi[:, m, :], dn_lo[:, m, cols], start=False, stop=False)
                                    ins = mm(bk_y[o][:], hbT_lo[:, m, :], dn_hi[:, m, cols], start=False, stop=last)
                                ins.then_inc(unit_used[GU_UNITS + m], 1)

                        over_blocks(pe, body)

                phase(weight_sems + sems, program)

        def combine():
            with ExitStack() as ctx:
                YT = [sb(f"YT{s}", [P, TOP_K, D], F32, ctx) for s in range(4)]
                y_loaded = [[ctx.enter_context(nc.semaphore(f"y_loaded{s}_{k}")) for k in range(TOP_K)] for s in range(4)]
                sems = sum(y_loaded, [])
                sq = sb("sq_c", [P, D], F32, ctx)
                added, half_added, sumsq, mean, rstd = (
                    ctx.enter_context(nc.semaphore(n))
                    for n in ("y_added", "y_half_added", "sumsq_c", "mean_square_c", "rstd_c"))
                sems += [added, half_added, sumsq, mean, rstd]

                def program(block):
                    @block.sync
                    def _(sp):
                        for j in range(NT):
                            if j >= 4:
                                sp.wait_ge(added, j - 3)
                            for k in range(TOP_K):
                                sp.dma_start(YT[j % 4][:, k], y_view[j, :, k]).then_inc(y_loaded[j % 4][k], 16)

                    @block.scalar
                    def _(act):
                        for j in range(NT):
                            act.wait_ge(added, j + 1)
                            square_rows(act, sq, j, sumsq)

                    @block.gpsimd
                    def _(pool):
                        reset_state(pool, rstd)
                        row_rstds(pool, mean, rstd)

                    @block.vector
                    def _(dve):
                        for j in range(NT):
                            for k in range(TOP_K):
                                dve.wait_ge(y_loaded[j % 4][k], 16 * (j // 4 + 1))
                                ins = nc.vector.scalar_tensor_tensor(out=X[:, j, :], in0=YT[j % 4][:, k, :],
                                                                     scalar=Wtok[:, j, k:k + 1], in1=X[:, j, :],
                                                                     op0=ALU.mult, op1=ALU.add)
                                if k == 0:
                                    ins.then_inc(half_added, 1)
                                    dve.wait_ge(half_added, j + 1)
                            ins.then_inc(added, 1)
                        mean_squares(dve, sumsq, mean)

                phase(sems, program)

        def final():
            with ExitStack() as ctx:
                gain = sb("gain_f", [P, D], F32, ctx)
                sems = [ctx.enter_context(nc.semaphore(n)) for n in ("gain_f_loaded", "out_ready", "out_stored")]
                gain_loaded, out_ready, stored = sems

                def program(block):
                    @block.sync
                    def _(sp):
                        sp.dma_start(gain[:], final_norm.rearrange("(a d) -> a d", a=1).broadcast_to([P, D])
                                     ).then_inc(gain_loaded, 16)
                        for j in range(NT):
                            sp.wait_ge(out_ready, j + 1)
                            sp.dma_start(out_rows[:, j, :], X[:, j, :]).then_inc(stored, 16)
                        sp.wait_ge(stored, 16 * NT)

                    @block.vector
                    def _(dve):
                        dve.wait_ge(gain_loaded, 16)
                        for j in range(NT):
                            nc.vector.scalar_tensor_tensor(out=X[:, j, :], in0=X[:, j, :], scalar=row_rstd[:, j:j + 1],
                                                           in1=gain[:], op0=ALU.mult, op1=ALU.mult).then_inc(out_ready, 1)

                phase(sems, program)

        with nc.Fori(0, DEPTH) as L:
            with nc.Fori(0, HALVES) as half:
                mixer_half(L, half)
            moe(L)
            combine()
        final()


_INS = ["x", "attn_norm", "w_in", "w_gk_up", "b_gk", "gla_norm", "gmlp_norm", "w_spatial", "b_spatial", "w_conv",
        "w_out", "ffn_norm", "ffn_norm_col", "w_router_group", "b_router_group", "w_router_expert", "b_router_expert",
        "w_gate", "w_up", "w_down", "final_norm"]


def kernel(**inputs):
    import numpy as _np
    import concourse.bacc as _bacc
    from concourse import mybir as _mybir
    from concourse.bass_utils import run_bass_kernel_spmd as _run

    nc = _bacc.Bacc("TRN2", target_bir_lowering=False, num_devices=1)
    arrays, args = {}, []
    def col(w):
        return w.reshape(w.shape[0], -1, 128).transpose(0, 2, 1)
    lay = {"attn_norm": col, "ffn_norm_col": col, "b_gk": col, "gla_norm": col,
           "w_spatial": lambda w: w.transpose(0, 3, 1, 2), "b_spatial": lambda w: w.transpose(0, 2, 1),
           "w_conv": lambda w: w.reshape(w.shape[0], w.shape[1], -1, 128).transpose(0, 3, 2, 1),
           "w_router_group": lambda w: w.reshape(w.shape[0], -1, 128, w.shape[2]).transpose(0, 2, 1, 3),
           "w_router_expert": lambda w: w.reshape(w.shape[0], -1, 128, w.shape[2]).transpose(0, 2, 1, 3)}
    for name in _INS:
        a = _np.asarray(inputs[name.removesuffix("_col")])
        a = _np.ascontiguousarray(lay[name](a) if name in lay else a)
        arrays[f"in_{name}_dram"] = a
        args.append(nc.dram_tensor(f"in_{name}_dram", a.shape, _mybir.dt.from_np(a.dtype), kind="ExternalInput").ap())
    shape = inputs["x"].shape
    args.append(nc.dram_tensor("out_0_dram", shape, _mybir.dt.float32, kind="ExternalOutput").ap())
    build(nc, *args)
    r = _run(nc, [arrays], core_ids=[0])
    return r.results[0]["out_0_dram"]
```
